# Optimizing a Trainium2 kernel written in Bass

```python
import jax, jax.numpy as jnp
from jax import lax
import numpy as np

D_MODEL = 1024
BATCH = 1
SEQ = 512
DEPTH = 1

CHUNK = 64
Q_BLOCK = 128
GLA_HEADS = 4
GLA_DK = 128
GLA_DV = 256
GLA_RANK = 16
GLA_TAU = 16.0
GLA_QK = GLA_HEADS * GLA_DK
GLA_V = GLA_HEADS * GLA_DV
FOX_HEADS = 8
FOX_HD = 128
FOX_W = FOX_HEADS * FOX_HD
N_EXPERTS = 32
TOP_K = 4
D_FF = 1024
SWIGLU_LIMIT = 7.0
SWIGLU_ALPHA = 1.702
MOE_BLOCK = 128
LN_EPS = 1e-5
DEEPNORM_ALPHA = (2 * DEPTH) ** 0.25
DEEPNORM_BETA = (8 * DEPTH) ** -0.25
IN_SPLITS = (GLA_QK, GLA_QK, GLA_V, GLA_RANK, GLA_V, FOX_W, FOX_W, FOX_W, FOX_HEADS, D_MODEL, D_MODEL)
IN_COLS = sum(IN_SPLITS)

kernel_name = "gla_fox_gated_hybrid_moe_deepnorm"

def split_cols(t, sizes):
    idx, acc = [], 0
    for s in sizes[:-1]:
        acc += s
        idx.append(acc)
    return jnp.split(t, idx, axis=-1)

def layer_norm(x, g, b):
    xf = x.astype(jnp.float32)
    mu = jnp.mean(xf, axis=-1, keepdims=True)
    var = jnp.mean(jnp.square(xf - mu), axis=-1, keepdims=True)
    y = (xf - mu) * lax.rsqrt(var + LN_EPS) * g.astype(jnp.float32) + b.astype(jnp.float32)
    return y.astype(x.dtype)

def gla_branch(q, k, v, gate_low, r, w_gate_up, b_gate, g_norm):
    B, S, _ = q.shape
    n = S // CHUNK
    f32 = jnp.float32
    log_a = jax.nn.log_sigmoid((gate_low @ w_gate_up + b_gate).astype(f32)) / GLA_TAU
    qh = q.astype(f32).reshape(B, n, CHUNK, GLA_HEADS, GLA_DK) * (GLA_DK ** -0.5)
    kh = k.astype(f32).reshape(B, n, CHUNK, GLA_HEADS, GLA_DK)
    vh = v.astype(f32).reshape(B, n, CHUNK, GLA_HEADS, GLA_DV)
    la = log_a.reshape(B, n, CHUNK, GLA_HEADS, GLA_DK)
    cum = jnp.cumsum(la, axis=2)
    total = cum[:, :, -1]
    k_dec = kh * jnp.exp(total[:, :, None] - cum)
    d_state = jnp.einsum('bnchk,bnchv->bnhkv', k_dec, vh)

    def step(state, inp):
        dec, ds = inp
        new = jnp.exp(dec)[..., None] * state + ds
        return new, new

    s0 = jnp.zeros((B, GLA_HEADS, GLA_DK, GLA_DV), f32)
    _, states = lax.scan(step, s0, (jnp.moveaxis(total, 1, 0), jnp.moveaxis(d_state, 1, 0)))
    states = jnp.moveaxis(states, 0, 1)
    o = jnp.einsum('bnchk,bnhkv->bnchv', qh, states)
    o = o * lax.rsqrt(jnp.mean(jnp.square(o), axis=-1, keepdims=True) + LN_EPS) * g_norm.astype(f32)
    o = o.reshape(B, S, GLA_V) * jax.nn.silu(r.astype(f32))
    return o.astype(q.dtype)

def fox_branch(q, k, v, f_logit):
    B, S, _ = q.shape
    f32 = jnp.float32
    qh = q.reshape(B, S, FOX_HEADS, FOX_HD).transpose(0, 2, 1, 3)
    kh = k.reshape(B, S, FOX_HEADS, FOX_HD).transpose(0, 2, 1, 3)
    vh = v.reshape(B, S, FOX_HEADS, FOX_HD).transpose(0, 2, 1, 3)
    cum_f = jnp.cumsum(jax.nn.log_sigmoid(f_logit.astype(f32)), axis=1).transpose(0, 2, 1)
    scale = FOX_HD ** -0.5
    outs = []
    for i in range(S // Q_BLOCK):
        lo, hi = i * Q_BLOCK, (i + 1) * Q_BLOCK
        s = jnp.einsum('bhqd,bhkd->bhqk', qh[:, :, lo:hi], kh[:, :, :hi]).astype(f32) * scale
        s = s + cum_f[:, :, lo:hi, None] - cum_f[:, :, None, :hi]
        causal = (lo + jnp.arange(Q_BLOCK))[:, None] >= jnp.arange(hi)[None, :]
        p = jax.nn.softmax(jnp.where(causal, s, -jnp.inf), axis=-1)
        outs.append(jnp.einsum('bhqk,bhkd->bhqd', p.astype(vh.dtype), vh[:, :, :hi]))
    o = jnp.concatenate(outs, axis=2)
    return o.transpose(0, 2, 1, 3).reshape(B, S, FOX_W)

def moe_ffn(h, w_router, b_router, w_gate_up, b_gate_up, w_down, b_down):
    B, S, D = h.shape
    T = B * S
    xt = h.reshape(T, D)
    logits = (xt @ w_router + b_router).astype(jnp.float32)
    top_val, top_idx = lax.top_k(logits, TOP_K)
    gates = jax.nn.softmax(top_val, axis=-1)
    A = T * TOP_K
    flat_e = top_idx.reshape(A)
    flat_tok = jnp.repeat(jnp.arange(T, dtype=jnp.int32), TOP_K)
    flat_g = gates.reshape(A)
    order = jnp.argsort(flat_e)
    se = flat_e[order]
    counts = jnp.bincount(flat_e, length=N_EXPERTS)
    starts = jnp.cumsum(counts) - counts
    padded = (counts + MOE_BLOCK - 1) // MOE_BLOCK * MOE_BLOCK
    pad_ends = jnp.cumsum(padded)
    pad_starts = pad_ends - padded
    dest = pad_starts[se] + jnp.arange(A, dtype=jnp.int32) - starts[se]
    n_blocks = (A + N_EXPERTS * (MOE_BLOCK - 1) + MOE_BLOCK - 1) // MOE_BLOCK
    P = n_blocks * MOE_BLOCK
    slot_tok = jnp.zeros((P,), jnp.int32).at[dest].set(flat_tok[order])
    slot_g = jnp.zeros((P,), jnp.float32).at[dest].set(flat_g[order])
    blk_start = jnp.arange(n_blocks, dtype=jnp.int32) * MOE_BLOCK
    blk_e = jnp.minimum(jnp.sum(blk_start[:, None] >= pad_ends[None, :], axis=1), N_EXPERTS - 1)
    xs = xt[slot_tok].reshape(n_blocks, MOE_BLOCK, D)

    def expert_block(args):
        xb, e = args
        gu = xb @ w_gate_up[e] + b_gate_up[e]
        gate = jnp.minimum(gu[:, :D_FF], SWIGLU_LIMIT)
        up = jnp.clip(gu[:, D_FF:], -SWIGLU_LIMIT, SWIGLU_LIMIT)
        glu = gate * jax.nn.sigmoid(SWIGLU_ALPHA * gate)
        return ((up + 1.0) * glu) @ w_down[e] + b_down[e]

    ys = lax.map(expert_block, (xs, blk_e)).reshape(P, D)
    ys = ys * slot_g[:, None].astype(ys.dtype)
    out = jax.ops.segment_sum(ys, slot_tok, num_segments=T)
    return out.reshape(B, S, D)

def setup_inputs(seed: int = 0) -> dict:
    key = jax.random.key(seed)
    ks = jax.random.split(key, 24)
    L, D, E = DEPTH, D_MODEL, N_EXPERTS
    nrm = lambda k, shape: jax.random.normal(k, shape, jnp.float32)
    col_scale = np.ones((IN_COLS,), np.float32)
    off = 2 * GLA_QK
    col_scale[off:off + GLA_V] = DEEPNORM_BETA
    off = 2 * GLA_QK + GLA_V + GLA_RANK + GLA_V + 2 * FOX_W
    col_scale[off:off + FOX_W] = DEEPNORM_BETA
    w_in = nrm(ks[1], (L, D, IN_COLS)) * (D ** -0.5) * jnp.asarray(col_scale)
    return {
        "x": nrm(ks[0], (BATCH, SEQ, D)),
        "ln_in_g": 1.0 + 0.02 * nrm(ks[2], (D,)),
        "ln_in_b": 0.02 * nrm(ks[3], (D,)),
        "w_in": w_in,
        "w_gla_gate_up": nrm(ks[4], (L, GLA_RANK, GLA_QK)) * (GLA_RANK ** -0.5),
        "b_gla_gate": 1.0 + 0.5 * nrm(ks[5], (L, GLA_QK)),
        "g_gla_norm": 1.0 + 0.02 * nrm(ks[6], (L, GLA_DV)),
        "b_forget": 4.0 + 0.5 * nrm(ks[7], (L, FOX_HEADS)),
        "w_gla_proj": nrm(ks[8], (L, GLA_V, D)) * (GLA_V ** -0.5) * DEEPNORM_BETA,
        "w_fox_proj": nrm(ks[9], (L, FOX_W, D)) * (FOX_W ** -0.5) * DEEPNORM_BETA,
        "w_out": nrm(ks[10], (L, D, D)) * (D ** -0.5) * DEEPNORM_BETA,
        "ln_mix_g": 1.0 + 0.02 * nrm(ks[11], (L, D)),
        "ln_mix_b": 0.02 * nrm(ks[12], (L, D)),
        "w_router": nrm(ks[13], (L, D, E)) * (D ** -0.5),
        "b_router": 0.01 * nrm(ks[14], (L, E)),
        "w_gate_up": nrm(ks[15], (L, E, D, 2 * D_FF)) * (D ** -0.5) * DEEPNORM_BETA,
        "b_gate_up": 0.02 * nrm(ks[16], (L, E, 2 * D_FF)),
        "w_down": nrm(ks[17], (L, E, D_FF, D)) * (D_FF ** -0.5) * DEEPNORM_BETA,
        "b_down": 0.02 * nrm(ks[18], (L, E, D)),
        "ln_ffn_g": 1.0 + 0.02 * nrm(ks[19], (L, D)),
        "ln_ffn_b": 0.02 * nrm(ks[20], (L, D)),
    }

def reference(x, ln_in_g, ln_in_b, w_in, w_gla_gate_up, b_gla_gate, g_gla_norm, b_forget,
              w_gla_proj, w_fox_proj, w_out, ln_mix_g, ln_mix_b, w_router, b_router,
              w_gate_up, b_gate_up, w_down, b_down, ln_ffn_g, ln_ffn_b):
    h = layer_norm(x, ln_in_g, ln_in_b)
    for l in range(DEPTH):
        proj = h @ w_in[l]
        (gq, gk, gv, g_low, g_r, fq, fk, fv, f_f, z_gla, z_fox) = split_cols(proj, IN_SPLITS)
        y_gla = gla_branch(gq, gk, gv, g_low, g_r, w_gla_gate_up[l], b_gla_gate[l], g_gla_norm[l]) @ w_gla_proj[l]
        y_fox = fox_branch(fq, fk, fv, f_f + b_forget[l]) @ w_fox_proj[l]
        mixed = jax.nn.sigmoid(z_gla) * y_gla + jax.nn.sigmoid(z_fox) * y_fox
        h = layer_norm(DEEPNORM_ALPHA * h + mixed @ w_out[l], ln_mix_g[l], ln_mix_b[l])
        ffn = moe_ffn(h, w_router[l], b_router[l], w_gate_up[l], b_gate_up[l], w_down[l], b_down[l])
        h = layer_norm(DEEPNORM_ALPHA * h + ffn, ln_ffn_g[l], ln_ffn_b[l])
    return h


_drawn_inputs = setup_inputs


def setup_inputs(seed=0):
    import zlib

    import numpy as np

    out = dict(_drawn_inputs(seed))
    spreads = {}
    factors = {'w_gla_gate_up': 4.491,
     'g_gla_norm': 29.232,
     'b_forget': 57.112,
     'b_router': 6.92,
     'b_gate_up': 8.0,
     'b_down': 6.319,
     'ln_ffn_g': 8.042,
     'ln_ffn_b': 8.362,
     'w_fox_proj': 3.687}
    for name, (base, spread) in spreads.items():
        noise = np.random.default_rng([zlib.crc32(name.encode()), seed]).standard_normal(out[name].shape)
        drawn = base * np.exp(spread * noise) if base else spread * noise
        out[name] = __import__('jax').numpy.asarray(drawn.astype(out[name].dtype))
    for name, factor in factors.items():
        out[name] = (out[name] * factor).astype(out[name].dtype)
    return out
```

```python
import numpy as np

import concourse.bass as bass
from concourse import mybir

ALU = mybir.AluOpType
ACT = mybir.ActivationFunctionType
F32 = mybir.dt.float32
F32R = mybir.dt.float32r
BF16 = mybir.dt.bfloat16
I32 = mybir.dt.int32
U32 = mybir.dt.uint32
AX_X = mybir.AxisListType.X

P = 128
D = 1024
T = 512
TT = T // P
KT = D // P
CHUNK = 64
NCH = T // CHUNK
GH, GDK, GDV = 4, 128, 256
RANK = 16
TAU = 16.0
FH, FHD = 8, 128
E = 32
TOPK = 4
FF = 1024
LIMIT, SLOPE = 7.0, 1.702
EPS = 1e-5
ALPHA = 2.0 ** 0.25
BIG = 4096.0
OVMAX = 16

C_GQ, C_GK, C_GV = 0, GH * GDK, 2 * GH * GDK
C_LOW = C_GV + GH * GDV
C_R = C_LOW + RANK
C_FQ = C_R + GH * GDV
C_FK = C_FQ + FH * FHD
C_FV = C_FK + FH * FHD
C_FF = C_FV + FH * FHD
C_ZG = C_FF + FH
C_ZF = C_ZG + D

CW = 256
CE = KT * CW
RAW, SPL = 4, 3
XRAW, XSPL = 6, 4

DENSE = [("gk", j, "w_in", C_GK + CW * j) for j in range(2)]
DENSE += [("gv", j, "w_in", C_GV + CW * j) for j in range(4)]
DENSE += [("gq", j, "w_in", C_GQ + CW * j) for j in range(2)]
DENSE += [("gr", j, "w_in", C_R + CW * j) for j in range(4)]
DENSE += [("fv", j, "w_in", C_FV + CW * j) for j in range(4)]
for _j in range(4):
    DENSE += [("fq", _j, "w_in", C_FQ + CW * _j), ("fk", _j, "w_in", C_FK + CW * _j)]
DENSE += [("zg", j, "w_in", C_ZG + CW * j) for j in range(4)]
DENSE += [("zf", j, "w_in", C_ZF + CW * j) for j in range(4)]
NPROJ = len(DENSE)
DENSE += [("gp", j, "w_gla_proj", CW * j) for j in range(4)]
DENSE += [("fp", j, "w_fox_proj", CW * j) for j in range(4)]
NCD = len(DENSE)
DENSE += [("wo", j, "w_out", CW * j) for j in range(4)]
ND = len(DENSE)
BY_TOKEN = ("gk", "gv", "fv")
PLAIN = ("gp", "wo")
SPLIT_AT = {}
for _c, _d in enumerate(DENSE):
    if _d[0] not in PLAIN:
        SPLIT_AT[_c] = len(SPLIT_AT)
CHUNK_OF = {n: c for c, n in SPLIT_AT.items()}
NS = len(SPLIT_AT)
GLA0 = 16
FSLOT = 30
ATT0 = 36
ATT_SLOTS = 16

GUC, DNC = KT, 4
STEPC = GUC + DNC
NMAIN = E * STEPC
BODY_USES = STEPC // XRAW
PER_SLOT = ND // RAW

DVE_BODY_LINKS = 6
DVE_OV_LINKS = 2


class Steps:

    def __init__(self, engine, sem, start):
        self.engine, self.sem, self.start, self.used = engine, sem, start, 0

    def link(self, instruction):
        self.used += 1
        instruction.then_inc(self.sem, 1)
        self.engine.wait_ge(self.sem, self.start + self.used)

    def mark(self, instruction):
        self.used += 1
        instruction.then_inc(self.sem, 1)

    def join(self):
        self.engine.wait_ge(self.sem, self.start + self.used)


def build(nc, a, out):
    base = -(-nc.sbuf_base // 128) * 128

    def at(name, kb, shape, dtype=F32):
        return nc.alloc_sbuf_tensor_at(name, shape, dtype, offset=base + int(kb * 1024))

    raw = at("raw", 0, [P, RAW, CE])
    whi = at("whi", 32, [P, SPL, CE], F32R)
    wlo = at("wlo", 56, [P, SPL, CE], F32R)
    hT_hi = at("hT_hi", 80, [P, KT, T], F32R)
    hT_lo = at("hT_lo", 96, [P, KT, T], F32R)
    xt = at("xt", 112, [P, TT, D])
    lnin_g = at("lnin_g", 128, [P, D])
    lnin_b = at("lnin_b", 132, [P, D])
    gv = at("gv", 112, [P, TT, GH * GDV])
    gk = at("gk", 128, [P, TT, GH * GDK])
    gq = at("gq", 136, [P, GH, T])
    fqk = [at(f"fqk{b}", 112 + 8 * b, [P, 2, 2, T]) for b in range(2)]
    probs = at("probs", 128, [P, 2, T])
    probsT = at("probsT", 132, [P, 2, T])
    fneg = at("fneg", 136, [64, T], F32R)
    mix = at("mix", 112, [P, KT, T])
    szf = at("szf", 128, [P, KT, T])
    gr = at("gr", 144, [P, KT, T])
    fv = at("fv", 160, [P, FH, TT, FHD])
    foxT = at("foxT", 176, [P, FH, T])
    la = at("la", 160, [P, TT, GH * GDK])
    gtmp = at("gtmp", 168, [P, 2, T])
    glT = at("glT", 172, [RANK + 1, T])
    w_up = at("w_up", 174, [RANK + 1, T])
    state = at("state", 176, [P, NCH, GDV])
    osq = at("osq", 184, [P, 2, T])
    orstd = at("orstd", 188, [P, T])
    otmp = at("otmp", 190, [P, T])
    ftmp = at("ftmp", 188, [64, T], F32R)
    bias_raw = at("bias_raw", 176, [P, 768])
    bias_hi = at("bias_hi", 179, [P, 768], F32R)
    bias_lo = at("bias_lo", 182, [P, 768], F32R)
    h2 = at("h2", 80, [P, TT, D])
    lnmix_g = at("lnmix_g", 96, [P, D])
    lnmix_b = at("lnmix_b", 100, [P, D])
    h2T = at("h2T", 128, [P, KT, T])
    posm = at("posm", 104, [P, TT, E + 2])
    vals = at("vals", 105, [P, TT, E + 2, 4])
    logits = at("logits", 112, [P, TT, E])
    top_v = at("top_v", 113, [P, TT, 8])
    top_i = at("top_i", 113.25, [P, TT, 8], U32)
    top_f = at("top_f", 113.5, [P, TT, 8])
    gate_e = at("gate_e", 113.75, [P, TT, TOPK])
    gate_s = at("gate_s", 114, [P, TT])
    gate_r = at("gate_r", 114.25, [P, TT])
    gates = at("gates", 114.5, [P, TT, TOPK])
    hot = at("hot", 115, [P, 3, TT, E, TOPK])
    member3 = at("member3", 121, [P, TT, 3 * E])
    posb = at("posb", 122.5, [P, TT, E])
    ovflag = at("ovflag", 123, [3 * E, 1])
    ovpre = at("ovpre", 123.25, [3 * E, 1])
    ovhot = at("ovhot", 123.5, [3 * E, OVMAX])
    ovtab = at("ovtab", 108, [1, 2 * OVMAX + 1], I32)
    lnffn_g = at("lnffn_g", 120, [P, D])
    lnffn_b = at("lnffn_b", 172, [P, D])
    raw2 = at("raw2", 128, [P, XRAW - RAW, CE])
    whi2 = at("whi2", 96, [P, CE], F32R)
    wlo2 = at("wlo2", 112, [P, CE], F32R)
    slots = at("slots", 124, [P, TT, P])
    xg = at("xg", 144, [P, D])
    xT_hi = at("xT_hi", 148, [P, KT, P], F32R)
    xT_lo = at("xT_lo", 152, [P, KT, P], F32R)
    gate_t = at("gate_t", 156, [P, FF])
    up_t = at("up_t", 160, [P, FF])
    act_t = at("act_t", 164, [P, FF])
    aT = at("aT", 168, [P, KT, P])
    y_t = at("y_t", 176, [P, D])
    bgu = at("bgu", 180, [2, 2 * FF], F32R)
    bdn = at("bdn", 188, [2, D], F32R)
    yrows = at("yrows", 0, [P, TT, TOPK * D])
    ident = at("ident", 192, [P, P])
    suffix = at("suffix", 192.5, [P, P])
    incl = at("incl", 193, [P, P])
    strict = at("strict", 193.5, [P, P])
    ones = at("ones", 194, [P, P])
    ones_dv = at("ones_dv", 194.5, [P, P])
    negmask = at("negmask", 195, [P, P], BF16)
    ident_b = at("ident_b", 195.25, [P, P], BF16)
    iota = at("iota", 195.5, [P, T])
    w_rt = at("w_rt", 197.5, [P, KT, E])
    sm_raw = at("sm_raw", 198.5, [P, KT, RANK + FH])
    sm_hi = at("sm_hi", 199.25, [P, KT, RANK + FH], F32R)
    sm_lo = at("sm_lo", 200, [P, KT, RANK + FH], F32R)
    ones_r = at("ones_r", 200.75, [2, P], F32R)
    b_rt = at("b_rt", 201.25, [P, E])
    glf = at("glf", 201.375, [P, TT, RANK + FH])
    small = at("small", 201.75, [P, 256])
    sel = at("sel", 203, [64, FH * P], F32R)

    cut = [0]

    def vec(*shape):
        n = int(np.prod(shape))
        view = small[:, cut[0]:cut[0] + n]
        cut[0] += n
        if len(shape) == 1:
            return view
        names = "abc"[:len(shape)]
        return view.rearrange(f"p ({' '.join(names)}) -> p {' '.join(names)}", **dict(zip(names, shape)))

    stats = vec(TT, 12)
    mv = vec(TT, 2)
    rstd = vec(TT)
    decay = vec(GH, NCH)
    fcum = vec(TT, FH)
    lsf = vec(TT, FH)
    lst = vec(TT, FH)
    b_f = vec(FH)
    g_norm = vec(2)
    chunk_sel = vec(2)
    smax, snmax, ssum, srec = vec(2), vec(2), vec(2), vec(2)
    tokcode = vec(TT)
    destcode = vec(TT, TOPK)
    queue = vec(4, 2)
    ovexp = vec(1)
    eps_c = vec(1)
    ovbase = vec(1)
    gidx = at("gidx", 202.75, [P, 1], U32)
    didx = at("didx", 202.875, [P, 1], U32)

    psA = nc.alloc_psum_tensor("psA", [P, 4, 512], F32)
    psX = nc.alloc_psum_tensor("psX", [P, 4, 512], F32)
    psD, psT = psX[:, 0:2, :], psX[:, 2:4, :]

    h_dram = nc.dram_tensor("h_dram", [T, D], F32, kind="Internal").ap()
    h2_dram = nc.dram_tensor("h2_dram", [T, D], F32, kind="Internal").ap()
    y_dram = nc.dram_tensor("y_dram", [T * TOPK, D], F32, kind="Internal").ap()
    bgu_dram = nc.dram_tensor("bgu_dram", [2, E * 2 * FF], F32R, kind="Internal").ap()
    bdn_dram = nc.dram_tensor("bdn_dram", [2, E * D], F32R, kind="Internal").ap()
    bgu_rows = bgu_dram.rearrange("s (e c) -> s e c", e=E)
    bdn_rows = bdn_dram.rearrange("s (e c) -> s e c", e=E)

    S = nc.alloc_semaphore
    const_ready = S("const_ready")
    x_in = [S(f"x_in{t}") for t in range(TT)]
    lnin_in, small_in, params_in, bias_in = S("lnin_in"), S("small_in"), S("params_in"), S("bias_in")
    lnmix_in, lnffn_in = S("lnmix_in"), S("lnffn_in")
    raw_in = [S(f"raw_in{s}") for s in range(XRAW)]
    hi_ready, lo_ready = S("hi_ready"), S("lo_ready")
    small_hi, small_lo = S("small_hi"), S("small_lo")
    bias_hi_s, bias_lo_s, bias_out = S("bias_hi_s"), S("bias_lo_s"), S("bias_out")
    h_norm, h_turned, hT_hi_s, hT_lo_s, h_out, h_back = (
        S("h_norm"), S("h_turned"), S("hT_hi_s"), S("hT_lo_s"), S("h_out"), S("h_back"))
    half_done = S("half_done")
    act_half, dve_half = S("act_half"), S("dve_half")
    small_done, small_evac = S("small_done"), S("small_evac")
    glT_done, glT_evac = S("glT_done"), S("glT_evac")
    gate_pre, la_ln, la_ready = S("gate_pre"), S("la_ln"), S("la_ready")
    suf_done, kd_exp, kd_mul = S("suf_done"), S("kd_exp"), S("kd_mul")
    tot_done, dec_ready, lsf_ln, lsf_ready = S("tot_done"), S("dec_ready"), S("lsf_ln"), S("lsf_ready")
    lsf_in = S("lsf_in")
    ds_done, st_ready, go_done, gsq_done, gms_done, gla_out = (
        S("ds_done"), S("st_ready"), S("go_done"), S("gsq_done"), S("gms_done"), S("gla_out"))
    f_done, f_evac, fneg_zero, fneg_hi, fneg_lo = (
        S("f_done"), S("f_evac"), S("fneg_zero"), S("fneg_hi"), S("fneg_lo"))
    at_score, at_max, at_exp, at_prob, at_turn, at_probT, at_out, at_evac = (
        S("at_score"), S("at_max"), S("at_exp"), S("at_prob"), S("at_turn"), S("at_probT"),
        S("at_out"), S("at_evac"))
    h2_norm, h2_turned, h2T_evac, h2_out = S("h2_norm"), S("h2_turned"), S("h2T_evac"), S("h2_out")
    lg_done, ge_in, ge_exp = S("lg_done"), S("ge_in"), S("ge_exp")
    mem_ready, pos_done, flag_ready, pre_done, ovhot_ready, ovlist_done, routed = (
        S("mem_ready"), S("pos_done"), S("flag_ready"), S("pre_done"), S("ovhot_ready"),
        S("ovlist_done"), S("routed"))
    slot_ready, tab_done, tab_ready = S("slot_ready"), S("tab_done"), S("tab_ready")
    xg_in, xt_done, xT_hi_s, xT_lo_s = S("xg_in"), S("xt_done"), S("xT_hi_s"), S("xT_lo_s")
    gu_used, dn_used = S("gu_used"), S("dn_used")
    fox_hi, fox_lo = S("fox_hi"), S("fox_lo")
    wo_done, wo_evac = S("wo_done"), S("wo_evac")
    gu_done, gate_min, sig_done, act_ready = S("gu_done"), S("gate_min"), S("sig_done"), S("act_ready")
    aturn_done, aT_ready = S("aturn_done"), S("aT_ready")
    dn_done, y_ready, y_out = S("dn_done"), S("y_ready"), S("y_out")
    gathers, scatters = S("gathers"), S("scatters")
    bgu_in, bdn_in = S("bgu_in"), S("bdn_in")
    yrows_in = [S(f"yrows_in{t}") for t in range(TT)]
    fin_ready, fin_out = S("fin_ready"), S("fin_out")
    dve_seq, act_seq, fin_seq = S("dve_seq"), S("act_seq"), S("fin_seq")
    var_ready, std_ready, gsqrt_done = S("var_ready"), S("std_ready"), S("gsqrt_done")

    h_tiles = h_dram.rearrange("(t p) d -> t p d", p=P)
    h2_tiles = h2_dram.rearrange("(t p) d -> t p d", p=P)
    x_tiles = a["x"][0].rearrange("(t p) d -> t p d", p=P)
    out_tiles = out[0].rearrange("(t p) d -> t p d", p=P)
    y_tiles = y_dram.rearrange("(t p k) d -> t p (k d)", p=P, k=TOPK)
    w_gu, w_dn = a["w_gate_up"][0], a["w_down"][0]

    def bcast(vector, n=D):
        return vector.rearrange("(a d) -> a d", a=1).to_broadcast([P, n])

    def raw_wait(eng, c):
        eng.wait_ge(raw_in[c % RAW], 16 * (c // RAW + 1))

    def xraw_wait(eng, slot, uses):
        eng.wait_ge(raw_in[slot], 16 * ((PER_SLOT if slot < RAW else 0) + uses))

    def evac_sem(c):
        return act_half if c < NPROJ else dve_half

    def evac_count(c):
        return 2 * (c + 1) if c < NPROJ else 2 * (c - NPROJ + 1)

    def body_slot(c):
        return (GUC + c) % XRAW

    def body_uses(i, c):
        return BODY_USES * (i - 1) + (GUC + c) // XRAW + 1

    def xraw(slot):
        return raw[:, slot, :] if slot < RAW else raw2[:, slot - RAW, :]

    def xsplit(c):
        ss = c % XSPL
        return (whi[:, ss, :], wlo[:, ss, :]) if ss < SPL else (whi2[:], wlo2[:])

    def attention_tiles(s):
        pair, q = divmod(s, TT)
        return [(2 * pair, q), (2 * pair + 1, TT - 1 - q)]

    def chunk_state(n):
        col = (n // 2 % 2) * GDV
        return psX[:, 2 * (n % 2) + n // 4, col:col + GDV]

    block = nc.Block()
    block.__enter__()

    @block.sync
    def _(sp):
        for t in range(TT):
            sp.dma_start(xt[:, t, :], x_tiles[t]).then_inc(x_in[t], 16)
        sources = {n: a[n][0] for n in ("w_in", "w_gla_proj", "w_fox_proj", "w_out")}
        for c, (kind, j, source, col) in enumerate(DENSE):
            if c >= RAW:
                o = c - RAW
                if o in SPLIT_AT:
                    sp.wait_ge(hi_ready, SPLIT_AT[o] + 1)
                    sp.wait_ge(lo_ready, SPLIT_AT[o] + 1)
                else:
                    sp.wait_ge(half_done, 2 * (o + 1))
            src = sources[source].rearrange("(k p) c -> p k c", p=P)[:, :, col:col + CW]
            sp.dma_start(raw[:, c % RAW, :].rearrange("p (k c) -> p k c", k=KT), src).then_inc(raw_in[c % RAW], 16)

        def load_gu(e, c, slot):
            sp.dma_start(xraw(slot), w_gu[e, c * P:(c + 1) * P, :]).then_inc(raw_in[slot], 16)

        def load_dn(e, q, slot):
            src = w_dn[e, 2 * q * P:2 * (q + 1) * P, :].rearrange("(k p) c -> p k c", p=P)
            sp.dma_start(xraw(slot).rearrange("p (k c) -> p k c", k=2), src).then_inc(raw_in[slot], 16)

        def after_gu(i, c):
            sp.wait_ge(hi_ready, NS + GUC * i + c + 1)
            sp.wait_ge(lo_ready, NS + GUC * i + c + 1)

        def after_dn(i, q):
            sp.wait_ge(dn_used, DNC * i + q + 1)

        for c in range(GUC):
            if c < RAW:
                sp.wait_ge(wo_done, TT)
            elif c < XRAW:
                sp.wait_ge(lg_done, TT)
            else:
                after_gu(0, c - XRAW)
            load_gu(0, c, c % XRAW)

        def body(i):
            for c in range(STEPC):
                if c >= XRAW:
                    after_gu(i, c - XRAW)
                elif isinstance(i, int):
                    after_gu(0, GUC - XRAW + c)
                elif c < 2:
                    after_gu(i - 1, XRAW + c)
                else:
                    after_dn(i - 2, c - 2)
                if c < GUC:
                    load_gu(i, c, body_slot(c))
                else:
                    load_dn(i - 1, c - GUC, body_slot(c))

        body(1)
        with sp.Fori(2, E) as i:
            body(i)
        for q in range(DNC):
            if q < 2:
                after_gu(E - 1, XRAW + q)
            else:
                after_dn(E - 2, q - 2)
            load_dn(E - 1, q, body_slot(q))
        sp.wait_ge(routed, 1)
        count = sp.value_load(ovtab[0:1, 2 * OVMAX:2 * OVMAX + 1], min_val=0, max_val=OVMAX)
        with sp.If(count > 0):
            with sp.Fori(0, count) as j:
                e = sp.value_load(ovtab[0:1, bass.ds(j, 1)], min_val=0, max_val=E - 1)
                sp.wait_ge(dn_used, DNC * (E + j))
                for c in range(STEPC):
                    if c >= XRAW:
                        after_gu(E + j, c - XRAW)
                    if c < GUC:
                        load_gu(e, c, c % XRAW)
                    else:
                        load_dn(e, c - GUC, c % XRAW)
        sp.wait_ge(fin_ready, 1)
        for t in range(TT):
            sp.dma_start(yrows[:, t, :], y_tiles[t]).then_inc(yrows_in[t], 16)
        for t in range(TT):
            sp.wait_ge(fin_ready, t + 2)
            sp.dma_start(out_tiles[t], h2[:, t, :]).then_inc(fin_out, 16)
        sp.wait_ge(fin_out, 16 * TT)

    @block.gpsimd
    def _(pool):
        g = nc.gpsimd
        marks = Steps(pool, const_ready, 0)
        for t, v in ((ident, 0.0), (ident_b, 0.0), (suffix, 1.0), (incl, 1.0), (strict, 1.0), (ones, 1.0),
                     (ones_dv, 1.0 / GDV), (negmask, 0.0), (glT, 1.0)):
            marks.mark(g.memset(t[:], v))
        for t in (ones_r, sel):
            marks.mark(g.memset(t[:].bitcast(F32), 1.0))
        marks.mark(g.memset(eps_c, EPS))
        marks.link(g.memset(chunk_sel, 0.0))
        for b in range(3):
            marks.link(g.memset(ovbase[E * b:E * (b + 1)], float(P * (b + 1))))
            marks.link(g.iota(ovexp[E * b:E * (b + 1)], [[0, 1]], base=0, channel_multiplier=1,
                              allow_small_or_imprecise_dtypes=True))
        marks.mark(g.iota(iota[:], [[1, T]], base=0, channel_multiplier=0, allow_small_or_imprecise_dtypes=True))
        marks.mark(g.iota(tokcode, [[P, TT]], base=-int(BIG), channel_multiplier=1,
                          allow_small_or_imprecise_dtypes=True))
        marks.mark(g.iota(destcode, [[TOPK * P, TT], [1, TOPK]], base=-int(BIG), channel_multiplier=TOPK,
                          allow_small_or_imprecise_dtypes=True))
        marks.join()
        sel_of = lambda t, pattern, op, fill, base_, mult: marks.mark(
            g.affine_select(out=t, in_=t, pattern=pattern, compare_op=op, fill=fill, base=base_,
                            channel_multiplier=mult))
        sel_of(ident[:], [[-1, P]], ALU.not_equal, 1.0, 0, 1)
        sel_of(suffix[:], [[-1, P]], ALU.is_gt, 0.0, 0, 1)
        sel_of(incl[:], [[1, P]], ALU.is_ge, 0.0, 0, -1)
        sel_of(strict[:], [[1, P]], ALU.is_gt, 0.0, 0, -1)
        sel_of(negmask[:], [[-1, P]], ALU.is_ge, -1e30, 0, 1)
        sel_of(ident_b[:], [[-1, P]], ALU.not_equal, 1.0, 0, 1)
        marks.join()
        for r in range(2):
            marks.link(g.affine_select(out=sel[32 * r:32 * (r + 1)].rearrange("p (h c) -> p h c", h=FH),
                                       in_=sel[32 * r:32 * (r + 1)].bitcast(F32).rearrange("p (h c) -> p h c", h=FH),
                                       pattern=[[1, FH], [0, P]], compare_op=ALU.is_equal, fill=0.0, base=0,
                                       channel_multiplier=-1))
        sel_of(glT[:], [[0, T]], ALU.is_gt, 1.0, RANK + 1, -1)
        marks.join()
        marks.link(g.memset(suffix[CHUNK:P, 0:CHUNK], 0.0))
        marks.link(g.memset(chunk_sel[0:CHUNK, 0:1], 1.0))
        marks.link(g.memset(chunk_sel[CHUNK:P, 1:2], 1.0))
        build.const_total = marks.used

        for t in range(TT):
            pool.wait_ge(h_norm, t + 1)
            g.dma_start(h_tiles[t], xt[:, t, :]).then_inc(h_out, 16)
        pool.wait_ge(bias_hi_s, 1)
        pool.wait_ge(bias_lo_s, 1)
        for s, part in enumerate((bias_hi, bias_lo)):
            g.dma_start(bgu_dram[s].rearrange("(p c) -> p c", p=P), part[:, 0:512]).then_inc(bias_out, 16)
            g.dma_start(bdn_dram[s].rearrange("(p c) -> p c", p=P), part[:, 512:768]).then_inc(bias_out, 16)
        pool.wait_ge(h_out, 16 * TT)
        pool.wait_ge(half_done, 2 * NCD)
        for t in range(TT):
            g.dma_start(h2[:, t, :], h_tiles[t]).then_inc(h_back, 16)
        g.dma_start(lnmix_g[:], bcast(a["ln_mix_g"][0])).then_inc(lnmix_in, 16)
        g.dma_start(lnmix_b[:], bcast(a["ln_mix_b"][0])).then_inc(lnmix_in, 16)
        pool.wait_ge(h2_norm, 1)
        pool.wait_ge(bias_out, 64)
        g.memset(xg[:], 0.0).then_inc(const_ready, 1)
        for t in range(TT):
            pool.wait_ge(h2_norm, t + 1)
            g.dma_start(h2_tiles[t], h2[:, t, :]).then_inc(h2_out, 16)
        pool.wait_ge(h2_out, 16 * TT)
        pool.wait_ge(const_ready, build.const_total + 1)

        token_bound, row_bound = pool.to_reg(T - 1), pool.to_reg(T * TOPK - 1)

        def gather(tables, turned):
            pool.wait_ge(tab_ready, tables)
            if turned is not None:
                pool.wait_ge(xt_done, turned)
            pool.sem_inc(gathers, 1)
            g.indirect_dma_start(xg[:], None, h2_dram, bass.IndirectOffsetOnAxis(ap=gidx[:, 0:1], axis=0),
                                 bounds_check=token_bound, oob_is_err=False).then_inc(xg_in, 16)

        def scatter(i):
            pool.wait_ge(y_ready, i + 1)
            pool.sem_inc(scatters, 1)
            g.indirect_dma_start(y_dram, bass.IndirectOffsetOnAxis(ap=didx[:, 0:1], axis=0), y_t[:], None,
                                 bounds_check=row_bound, oob_is_err=False).then_inc(y_out, 16)

        def load_bgu(i, e):
            g.dma_start(bgu[:], bgu_rows[:, e, :]).then_inc(bgu_in, 16)

        def load_bdn(i, e):
            g.dma_start(bdn[:], bdn_rows[:, e, :]).then_inc(bdn_in, 16)

        gather(1, None)
        load_bgu(0, 0)
        load_bdn(0, 0)
        pool.wait_ge(routed, 1)
        g.dma_start(lnffn_g[:], bcast(a["ln_ffn_g"][0])).then_inc(lnffn_in, 16)
        g.dma_start(lnffn_b[:], bcast(a["ln_ffn_b"][0])).then_inc(lnffn_in, 16)
        gather(2, 1)
        gather(3, 2)

        def body(i, last):
            pool.wait_ge(gu_done, i)
            load_bgu(i, i)
            if not last:
                gather(i + 3, i + 2)
            scatter(i - 1)
            load_bdn(i, i)

        with pool.Fori(1, E - 1) as i:
            body(i, False)
        body(E - 1, True)
        scatter(E - 1)
        count = pool.value_load(ovtab[0:1, 2 * OVMAX:2 * OVMAX + 1], min_val=0, max_val=OVMAX)
        with pool.If(count > 0):
            with pool.Fori(0, count) as j:
                e = pool.value_load(ovtab[0:1, bass.ds(j, 1)], min_val=0, max_val=E - 1)
                gather(E + 4 + j, E + 1 + j)
                pool.wait_ge(gu_done, E + j)
                load_bgu(j, e)
                pool.wait_ge(dn_done, E + j)
                load_bdn(j, e)
                scatter(E + j)

    @block.scalar
    def _(act):
        s_ = nc.scalar
        seq = Steps(act, act_seq, 0)
        act.dma_start(lnin_g[:], bcast(a["ln_in_g"])).then_inc(lnin_in, 16)
        act.dma_start(lnin_b[:], bcast(a["ln_in_b"])).then_inc(lnin_in, 16)
        w_in = a["w_in"][0].rearrange("(k p) c -> p k c", p=P)
        act.dma_start(sm_raw[:, :, 0:RANK], w_in[:, :, C_LOW:C_LOW + RANK]).then_inc(small_in, 16)
        act.dma_start(sm_raw[:, :, RANK:RANK + FH], w_in[:, :, C_FF:C_FF + FH]).then_inc(small_in, 16)
        act.dma_start(w_up[0:RANK, :], a["w_gla_gate_up"][0]).then_inc(params_in, 16)
        act.dma_start(w_up[RANK:RANK + 1, :], a["b_gla_gate"]).then_inc(params_in, 16)
        act.dma_start(b_f, bcast(a["b_forget"][0], FH)).then_inc(params_in, 16)
        with nc.allow_non_contiguous_dma(reason="256 gains onto partitions"):
            act.dma_start(g_norm, a["g_gla_norm"][0].rearrange("(c p) -> p c", p=P)).then_inc(params_in, 16)
        act.dma_start(w_rt[:], a["w_router"][0].rearrange("(k p) e -> p k e", p=P)).then_inc(params_in, 16)
        act.dma_start(b_rt[:], bcast(a["b_router"][0], E)).then_inc(params_in, 16)
        act.dma_start(bias_raw[:, 0:512], a["b_gate_up"][0].rearrange("e (q c) -> (e q) c", c=512)).then_inc(bias_in, 16)
        act.dma_start(bias_raw[:, 512:768], a["b_down"][0].rearrange("e (q c) -> (e q) c", c=256)).then_inc(bias_in, 16)

        def dense_hi(c):
            if c not in SPLIT_AT:
                return
            n = SPLIT_AT[c]
            raw_wait(act, c)
            if n >= SPL:
                act.wait_ge(half_done, 2 * (CHUNK_OF[n - SPL] + 1))
            s_.copy(whi[:, n % SPL, :], raw[:, c % RAW, :]).then_inc(hi_ready, 1)

        def h_hi(t):
            act.wait_ge(h_turned, t + 1)
            ps = psX[:, 2 * (t % 2):2 * (t % 2) + 2, :].rearrange("p b (k c) -> p (b k) c", k=4)
            s_.copy(hT_hi[:, :, t * P:(t + 1) * P], ps).then_inc(hT_hi_s, 1)

        def std(n):
            act.wait_ge(var_ready, n + 1)
            t = n % TT
            s_.activation(rstd[:, t:t + 1], mv[:, t, 1:2], ACT.Sqrt, bias=eps_c).then_inc(std_ready, 1)

        dense_hi(0)
        act.wait_ge(const_ready, build.const_total)
        std(0)
        for t in range(TT):
            if t + 1 < TT:
                std(t + 1)
            h_hi(t)
        dense_hi(1)
        act.wait_ge(small_in, 32)
        s_.copy(sm_hi[:], sm_raw[:]).then_inc(small_hi, 1)
        act.wait_ge(bias_in, 32)
        s_.copy(bias_hi[:], bias_raw[:]).then_inc(bias_hi_s, 1)

        def evacuate(c, half):
            kind, j = DENSE[c][:2]
            act.wait_ge(half_done, 2 * c + half + 1)
            bank = 2 * (c % 2) + half
            if kind in BY_TOKEN:
                if kind == "gv" and half == 0:
                    act.wait_ge(h_out, 16 * TT)
                for u in range(2):
                    t = 2 * half + u
                    src = psA[:, bank, u * CW:(u + 1) * CW]
                    if kind == "fv":
                        ins = s_.copy(fv[:, 2 * j:2 * j + 2, t, :], src.rearrange("p (h c) -> p h c", h=2))
                    else:
                        ins = s_.copy({"gk": gk, "gv": gv}[kind][:, t, j * CW:(j + 1) * CW], src)
            else:
                i = 2 * j + half
                src = psA[:, bank, :]
                if kind == "gq":
                    ins = s_.activation(gq[:, i, :], src, ACT.Copy, scale=float(GDK) ** -0.5)
                elif kind == "gr":
                    ins = s_.activation(gr[:, i, :], src, ACT.Silu)
                elif kind == "fq":
                    ins = s_.activation(fqk[j % 2][:, 0, half, :], src, ACT.Copy, scale=float(FHD) ** -0.5)
                elif kind == "fk":
                    ins = s_.copy(fqk[j % 2][:, 1, half, :], src)
                elif kind == "zg":
                    ins = s_.activation(mix[:, i, :], src, ACT.Sigmoid)
                else:
                    ins = s_.activation(szf[:, i, :], src, ACT.Sigmoid)
            ins.then_inc(act_half, 1)

        def log_sigmoid_tail(dst, src):
            seq.link(s_.activation(dst, src, ACT.Abs))
            seq.link(s_.activation(dst, dst, ACT.Exp, scale=-1.0))
            return s_.activation(dst, dst, ACT.Ln, bias=1.0)

        def hook(s):
            if s == 1:
                act.wait_ge(small_done, 1)
                s_.copy(glf[:], psX[:, 2, 0:TT * (RANK + FH)].rearrange("p (t c) -> p t c", t=TT)).then_inc(small_evac, 1)
            if s == 2:
                act.wait_ge(glT_done, 1)
                s_.copy(glT[0:RANK, :], psX[0:RANK, 3, :]).then_inc(glT_evac, 1)
            if s in (3, 4):
                for b in range(2):
                    t = 2 * (s - 3) + b
                    act.wait_ge(gate_pre, t + 1)
                    if t >= 2:
                        act.wait_ge(la_ready, t - 1)
                    log_sigmoid_tail(gtmp[:, b, :], psX[:, t, :]).then_inc(la_ln, 1)
            if s in (5, 6):
                for b in range(2):
                    t = 2 * (s - 5) + b
                    act.wait_ge(suf_done, t + 1)
                    act.wait_ge(la_ready, TT if t < 2 else TT)
                    if t >= 2:
                        act.wait_ge(kd_mul, t - 1)
                    s_.activation(gtmp[:, b, :], psX[:, t, :], ACT.Exp, scale=1.0 / TAU).then_inc(kd_exp, 1)
            if s == 7:
                act.wait_ge(tot_done, 1)
                s_.activation(decay, psX[:, 0, 0:GH * NCH].rearrange("p (h n) -> p h n", h=GH), ACT.Exp,
                              scale=1.0 / TAU).then_inc(dec_ready, 1)
            if s == 8:
                act.wait_ge(lsf_in, 1)
                log_sigmoid_tail(lst, lsf).then_inc(lsf_ln, 1)
            if GLA0 <= s < GLA0 + 3 * GH and (s - GLA0) % 3 == 1:
                h = (s - GLA0) // 3
                act.wait_ge(go_done, h + 1)
                s_.activation(osq[:], psX[:, 0:2, :], ACT.Square).then_inc(gsq_done, 1)
            if GLA0 <= s < GLA0 + 3 * GH and (s - GLA0) % 3 == 2:
                h = (s - GLA0) // 3
                act.wait_ge(gms_done, h + 1)
                s_.activation(orstd[:], psX[:, 2, :], ACT.Sqrt, bias=eps_c).then_inc(gsqrt_done, 1)
            if s == FSLOT:
                act.wait_ge(f_done, 1)
                s_.copy(fcum, psX[:, 0, 0:TT * FH].rearrange("p (t h) -> p t h", t=TT)).then_inc(f_evac, 1)
                act.wait_ge(fneg_zero, 1)
                s_.activation(fneg[0:FH], psX[0:FH, 1, :], ACT.Copy, scale=-1.0)
                s_.activation(ftmp[32:32 + FH], psX[32:32 + FH, 1, :], ACT.Copy, scale=-1.0).then_inc(fneg_hi, 1)
            q = s - ATT0
            if 2 <= q < ATT_SLOTS + 2:
                for b, (h, t) in enumerate(attention_tiles(q - 2)):
                    act.wait_ge(at_out, 2 * (q - 2) + b + 1)
                    s_.copy(foxT[:, h, t * P:(t + 1) * P], psX[:, 2 + b, 0:P]).then_inc(at_evac, 1)
            if 0 <= q < ATT_SLOTS:
                for b, (h, t) in enumerate(attention_tiles(q)):
                    act.wait_ge(at_max, 2 * q + b + 1)
                    row = probs[:, b, 0:P * (t + 1)]
                    s_.activation(row, row, ACT.Exp, bias=snmax[:, b:b + 1],
                                  accum_out=ssum[:, b:b + 1]).then_inc(at_exp, 1)
            if 1 <= q < ATT_SLOTS + 1:
                for b, (h, t) in enumerate(attention_tiles(q - 1)):
                    act.wait_ge(at_turn, 2 * (q - 1) + b + 1)
                    n = P * (t + 1)
                    s_.copy(probsT[:, b, 0:n], psX[:, 2 + b, 0:n]).then_inc(at_probT, 1)

        for c in range(NPROJ):
            dense_hi(c + 2)
            for half in range(2):
                evacuate(c, half)
                hook(2 * c + half)
        act.wait_ge(half_done, 2 * NPROJ)
        act.wait_ge(at_evac, 2 * ATT_SLOTS)
        for u in range(4):
            pair = slice(2 * u, 2 * u + 2)
            s_.copy(hT_hi[:, pair, :], foxT[:, pair, :]).then_inc(fox_hi, 1)
        for c in range(NPROJ + 2, NCD):
            dense_hi(c)

        def expert_hi(i, c, slot, uses):
            xraw_wait(act, slot, uses)
            if isinstance(i, int) and i == 0 and c < XSPL:
                if c < SPL:
                    act.wait_ge(half_done, 2 * (CHUNK_OF[NS - SPL + c] + 1))
            else:
                act.wait_ge(gu_used, GUC * i + c - XSPL + 1)
            s_.copy(xsplit(c)[0], xraw(slot)).then_inc(hi_ready, 1)

        for t in range(TT):
            std(TT + t)
        for t in range(TT):
            act.wait_ge(h2_turned, t + 1)
            ps = psX[:, 2 * (t % 2):2 * (t % 2) + 2, :].rearrange("p b (k c) -> p (b k) c", k=4)
            s_.copy(h2T[:, :, t * P:(t + 1) * P], ps).then_inc(h2T_evac, 1)
        act.wait_ge(ge_in, 1)
        s_.activation(gate_e[:], gate_e[:], ACT.Exp).then_inc(ge_exp, 1)
        for c in range(XSPL):
            expert_hi(0, c, c, 1)

        def turned_hi(done, count, dst, sem):
            act.wait_ge(done, count)
            ps = psT.rearrange("p b (k c) -> p (b k) c", k=4)
            s_.copy(dst[:], ps).then_inc(sem, 1)

        def sigmoid(i):
            act.wait_ge(gate_min, i + 1)
            s_.activation(act_t[:], gate_t[:], ACT.Sigmoid, scale=SLOPE).then_inc(sig_done, 1)

        def y_evac(i, free):
            act.wait_ge(dn_done, i + 1)
            act.wait_ge(tab_ready, free)
            s_.activation(y_t[:], psD.rearrange("p b c -> p (b c)"), ACT.Copy,
                          scale=queue[:, 0, 1:2]).then_inc(y_ready, 1)

        turned_hi(xt_done, 1, xT_hi, xT_hi_s)

        def half_step(i, uses_of, slot_of):
            for c in range(XSPL, GUC):
                expert_hi(i, c, slot_of(c), uses_of(c))
            sigmoid(i)

        half_step(0, lambda c: c // XRAW + 1, lambda c: c % XRAW)
        turned_hi(xt_done, 2, xT_hi, xT_hi_s)
        for c in range(XSPL):
            expert_hi(1, c, body_slot(c), body_uses(1, c))
        turned_hi(aturn_done, 1, aT, aT_ready)

        def body(i, last):
            half_step(i, lambda c: body_uses(i, c), body_slot)
            turned_hi(xt_done, i + 2, xT_hi, xT_hi_s)
            if not last:
                for c in range(XSPL):
                    expert_hi(i + 1, c, body_slot(c), body_uses(i + 1, c))
            y_evac(i - 1, i + 3)
            turned_hi(aturn_done, i + 1, aT, aT_ready)

        with act.Fori(1, E - 1) as i:
            body(i, False)
        body(E - 1, True)
        y_evac(E - 1, E + 3)
        act.wait_ge(routed, 1)
        count = act.value_load(ovtab[0:1, 2 * OVMAX:2 * OVMAX + 1], min_val=0, max_val=OVMAX)
        with act.If(count > 0):
            with act.Fori(0, count) as j:
                turned_hi(xt_done, E + 2 + j, xT_hi, xT_hi_s)
                for c in range(GUC):
                    expert_hi(E + j, c, c % XRAW, NMAIN // XRAW + BODY_USES * j + c // XRAW + 1)
                sigmoid(E + j)
                turned_hi(aturn_done, E + 1 + j, aT, aT_ready)
                y_evac(E + j, E + 4 + j)
        for t in range(TT):
            std(2 * TT + t)

    @block.vector
    def _(dve):
        v = nc.vector
        seq = Steps(dve, dve_seq, 0)

        def norm_stats(t, row, chain):
            chain.mark(v.bn_stats(stats[:, t, 0:6], row[:, 0:512]))
            chain.link(v.bn_stats(stats[:, t, 6:12], row[:, 512:1024]))
            v.bn_aggr(mv[:, t, :], stats[:, t, :]).then_inc(var_ready, 1)

        def norm_apply(n, t, row, gain, offset, chain):
            dve.wait_ge(std_ready, n + 1)
            chain.link(v.reciprocal(rstd[:, t:t + 1], rstd[:, t:t + 1]))
            chain.link(v.scalar_tensor_tensor(row, row, mv[:, t, 0:1], gain, ALU.subtract, ALU.mult))
            return v.scalar_tensor_tensor(row, row, rstd[:, t:t + 1], offset, ALU.mult, ALU.add)

        def dense_lo(c):
            if c not in SPLIT_AT:
                return
            n = SPLIT_AT[c]
            dve.wait_ge(hi_ready, n + 1)
            v.tensor_tensor(wlo[:, n % SPL, :], raw[:, c % RAW, :], whi[:, n % SPL, :].bitcast(F32),
                            ALU.subtract).then_inc(lo_ready, 1)

        def h_lo(t):
            dve.wait_ge(hT_hi_s, t + 1)
            ps = psX[:, 2 * (t % 2):2 * (t % 2) + 2, :].rearrange("p b (k c) -> p (b k) c", k=4)
            cols = slice(t * P, (t + 1) * P)
            v.tensor_tensor(hT_lo[:, :, cols], ps, hT_hi[:, :, cols].bitcast(F32), ALU.subtract).then_inc(hT_lo_s, 1)

        dve.wait_ge(lnin_in, 32)
        for t in range(TT + 1):
            if t < TT:
                dve.wait_ge(x_in[t], 16)
                norm_stats(t, xt[:, t, :], seq)
            if t >= 1:
                norm_apply(t - 1, t - 1, xt[:, t - 1, :], lnin_g[:], lnin_b[:], seq).then_inc(h_norm, 1)
            if t >= 2:
                h_lo(t - 2)
            if t == 1:
                dense_lo(0)
        h_lo(TT - 1)
        dense_lo(1)
        dve.wait_ge(small_hi, 1)
        v.tensor_tensor(sm_lo[:], sm_raw[:], sm_hi[:].bitcast(F32), ALU.subtract).then_inc(small_lo, 1)
        dve.wait_ge(bias_hi_s, 1)
        v.tensor_tensor(bias_lo[:], bias_raw[:], bias_hi[:].bitcast(F32), ALU.subtract).then_inc(bias_lo_s, 1)

        def hook(s):
            if s in (3, 4):
                for b in range(2):
                    t = 2 * (s - 3) + b
                    dve.wait_ge(la_ln, t + 1)
                    v.scalar_tensor_tensor(la[:, t, :], psX[:, t, :], 0.0, gtmp[:, b, :], ALU.min,
                                           ALU.subtract).then_inc(la_ready, 1)
            if s in (5, 6):
                for b in range(2):
                    t = 2 * (s - 5) + b
                    dve.wait_ge(kd_exp, t + 1)
                    dve.wait_ge(act_half, 4)
                    v.tensor_tensor(gk[:, t, :], gk[:, t, :], gtmp[:, b, :], ALU.mult).then_inc(kd_mul, 1)
            if s == 8:
                dve.wait_ge(small_evac, 1)
                dve.wait_ge(params_in, 96)
                for t in range(TT):
                    ins = v.tensor_tensor(lsf[:, t, :], glf[:, t, RANK:RANK + FH], b_f, ALU.add)
                ins.then_inc(lsf_in, 1)
                dve.wait_ge(lsf_ln, 1)
                v.scalar_tensor_tensor(lsf, lsf, 0.0, lst, ALU.min, ALU.subtract).then_inc(lsf_ready, 1)
            if GLA0 <= s < GLA0 + 3 * GH:
                h, part = divmod(s - GLA0, 3)
                if part == 0:
                    dve.wait_ge(ds_done, h + 1)
                    dve.wait_ge(dec_ready, 1)
                    if h == 0:
                        dve.wait_ge(bias_out, 64)
                    for n in range(NCH):
                        ds = chunk_state(n)
                        if n == 0:
                            seq.link(v.tensor_copy(state[:, 0, :], ds))
                        else:
                            ins = v.scalar_tensor_tensor(state[:, n, :], state[:, n - 1, :], decay[:, h, n:n + 1],
                                                         ds, ALU.mult, ALU.add)
                            if n < NCH - 1:
                                seq.link(ins)
                    ins.then_inc(st_ready, 1)
                if part == 2:
                    dve.wait_ge(gms_done, h + 1)
                    dve.wait_ge(act_half, 2 * (8 + h + 1))
                    dve.wait_ge(gsqrt_done, h + 1)
                    seq.link(v.reciprocal(orstd[:], orstd[:]))
                    for half in range(2):
                        seq.link(v.scalar_tensor_tensor(otmp[:], psX[:, half, :], g_norm[:, half:half + 1], orstd[:],
                                                        ALU.mult, ALU.mult))
                        ins = v.tensor_tensor(gr[:, 2 * h + half, :], gr[:, 2 * h + half, :], otmp[:], ALU.mult)
                        if half == 0:
                            seq.link(ins)
                    ins.then_inc(gla_out, 1)
            if s == FSLOT:
                dve.wait_ge(gla_out, GH)
                v.memset(fneg[:].bitcast(F32), 0.0).then_inc(fneg_zero, 1)
                dve.wait_ge(fneg_hi, 1)
                rows = slice(32, 32 + FH)
                v.scalar_tensor_tensor(fneg[rows], psX[rows, 1, :], -1.0, ftmp[rows].bitcast(F32), ALU.mult,
                                       ALU.subtract).then_inc(fneg_lo, 1)
            q = s - ATT0
            if 0 <= q < ATT_SLOTS:
                for b, (h, t) in enumerate(attention_tiles(q)):
                    n = P * (t + 1)
                    dve.wait_ge(at_score, 2 * q + b + 1)
                    dve.wait_ge(f_evac, 1)
                    if q >= 1:
                        dve.wait_ge(at_turn, 2 * (q - 1) + b + 1)
                    seq.link(v.tensor_scalar(probs[:, b, 0:n], psX[:, b, 0:n], fcum[:, t, h:h + 1], -3e38, ALU.add,
                                             ALU.max, accum_out=smax[:, b:b + 1]))
                    v.tensor_scalar(snmax[:, b:b + 1], smax[:, b:b + 1], -1.0, None, ALU.mult).then_inc(at_max, 1)
                for b, (h, t) in enumerate(attention_tiles(q)):
                    n = P * (t + 1)
                    dve.wait_ge(at_exp, 2 * q + b + 1)
                    seq.link(v.reciprocal(srec[:, b:b + 1], ssum[:, b:b + 1]))
                    v.tensor_scalar(probs[:, b, 0:n], probs[:, b, 0:n], srec[:, b:b + 1], None,
                                    ALU.mult).then_inc(at_prob, 1)

        for c in range(NPROJ):
            dense_lo(c + 2)
            for half in range(2):
                hook(2 * c + half)
        for u in range(4):
            dve.wait_ge(fox_hi, u + 1)
            pair = slice(2 * u, 2 * u + 2)
            v.tensor_tensor(hT_lo[:, pair, :], foxT[:, pair, :], hT_hi[:, pair, :].bitcast(F32),
                            ALU.subtract).then_inc(fox_lo, 1)
        for c in range(NPROJ, NCD):
            kind, j = DENSE[c][:2]
            dense_lo(c + 2)
            for half in range(2):
                i = 2 * j + half
                bank = 2 * (c % 2) + half
                dve.wait_ge(half_done, 2 * c + half + 1)
                if kind == "gp":
                    ins = v.tensor_tensor(mix[:, i, :], mix[:, i, :], psA[:, bank, :], ALU.mult)
                else:
                    seq.link(v.tensor_tensor(szf[:, i, :], szf[:, i, :], psA[:, bank, :], ALU.mult))
                    ins = v.tensor_tensor(mix[:, i, :], mix[:, i, :], szf[:, i, :], ALU.add)
                ins.then_inc(dve_half, 1)
        dve.wait_ge(h_back, 16 * TT)
        dve.wait_ge(lnmix_in, 32)
        for t in range(TT + 1):
            if t < TT:
                dve.wait_ge(wo_done, t + 1)
                product = psA[:, 2 * (t % 2):2 * (t % 2) + 2, :].rearrange("p b c -> p (b c)")
                v.scalar_tensor_tensor(h2[:, t, :], h2[:, t, :], ALPHA, product, ALU.mult,
                                       ALU.add).then_inc(wo_evac, 1)
                dve.wait_ge(wo_evac, t + 1)
                norm_stats(t, h2[:, t, :], seq)
            if t >= 1:
                norm_apply(TT + t - 1, t - 1, h2[:, t - 1, :], lnmix_g[:], lnmix_b[:], seq).then_inc(h2_norm, 1)

        def expert_lo(i, c, slot):
            dve.wait_ge(hi_ready, NS + GUC * i + c + 1)
            hi, lo = xsplit(c)
            v.tensor_tensor(lo, xraw(slot), hi.bitcast(F32), ALU.subtract).then_inc(lo_ready, 1)

        for t in range(TT):
            dve.wait_ge(lg_done, TT)
            seq.mark(v.tensor_tensor(logits[:, t, :], psA[:, 0, t * E:(t + 1) * E], b_rt[:], ALU.add))
        seq.join()
        for t in range(TT):
            seq.mark(v.max(top_v[:, t, :], logits[:, t, :]))
        seq.join()
        for t in range(TT):
            seq.mark(v.max_index(top_i[:, t, :], top_v[:, t, :], logits[:, t, :]))
            last = v.tensor_scalar(gate_e[:, t, :], top_v[:, t, 0:TOPK], top_v[:, t, 0:1], None, ALU.subtract)
        last.then_inc(ge_in, 1)
        seq.join()
        seq.link(v.tensor_copy(top_f[:], top_i[:]))
        dve.wait_ge(ge_exp, 1)
        seq.link(v.tensor_reduce(gate_s[:], gate_e[:], AX_X, ALU.add))
        seq.link(v.reciprocal(gate_r[:], gate_s[:]))
        for t in range(TT):
            seq.mark(v.tensor_scalar(gates[:, t, :], gate_e[:, t, :], gate_r[:, t:t + 1], None, ALU.mult))
        seq.join()
        dve.wait_ge(const_ready, build.const_total)
        for t in range(TT):
            for k in range(TOPK):
                idx = top_f[:, t, k:k + 1]
                seq.mark(v.tensor_scalar(hot[:, 0, t, :, k], iota[:, 0:E], idx, None, ALU.is_equal))
                seq.mark(v.tensor_scalar(hot[:, 1, t, :, k], iota[:, 0:E], idx, destcode[:, t, k:k + 1],
                                         ALU.is_equal, ALU.mult))
                seq.mark(v.tensor_scalar(hot[:, 2, t, :, k], iota[:, 0:E], idx, gates[:, t, k:k + 1],
                                         ALU.is_equal, ALU.mult))
        seq.mark(v.memset(vals[:], 0.0))
        seq.mark(v.memset(posm[:], -1.0))
        seq.join()
        seq.link(v.tensor_reduce(member3[:, :, 0:E], hot[:, 0], AX_X, ALU.add))
        v.tensor_copy(member3[:, :, E:2 * E], member3[:, :, 0:E])
        v.tensor_copy(member3[:, :, 2 * E:3 * E], member3[:, :, 0:E]).then_inc(mem_ready, 1)
        seq.mark(v.tensor_reduce(vals[:, :, 0:E, 1], hot[:, 1], AX_X, ALU.add))
        seq.mark(v.tensor_reduce(vals[:, :, 0:E, 2], hot[:, 2], AX_X, ALU.add))
        for t in range(TT):
            seq.mark(v.tensor_scalar(vals[:, t, 0:E, 0], member3[:, t, 0:E], tokcode[:, t:t + 1], None, ALU.mult))
        seq.link(v.tensor_scalar(posb[:], member3[:, :, 0:E], BIG, -BIG, ALU.mult, ALU.add))
        dve.wait_ge(pos_done, 1)
        seq.link(v.tensor_tensor(posm[:, :, 0:E], posb[:],
                                 psA[:, 1, 0:TT * E].rearrange("p (t e) -> p t e", t=TT), ALU.add))

        def slot_rows(e, rows):
            for t in range(TT):
                ins = v.tensor_scalar(slots[:, t, :], rows, posm[:, t, e], None, ALU.is_equal)
            ins.then_inc(slot_ready, 1)

        def shift_queue(chain):
            chain.join()
            chain.link(v.tensor_copy(queue[:, 0, :], queue[:, 1, :]))
            chain.link(v.tensor_copy(queue[:, 1, :], queue[:, 2, :]))
            chain.link(v.tensor_copy(queue[:, 2, :], queue[:, 3, :]))

        def take_table(x, chain):
            dve.wait_ge(tab_done, x + 1)
            if not (isinstance(x, int) and x == 0):
                dve.wait_ge(xg_in, 16 * x)
            chain.link(v.tensor_copy(queue[:, 3, :], psD[:, 0, 1:3]))
            chain.mark(v.tensor_scalar(didx[:], queue[:, 0, 0:1], BIG, None, ALU.add))
            v.tensor_scalar(gidx[:], psD[:, 0, 0:1], BIG, None, ALU.add).then_inc(tab_ready, 1)

        slot_rows(slice(0, 1), iota[:, 0:P])
        seq.link(v.memset(queue, 0.0))
        take_table(0, seq)
        seq.link(v.tensor_scalar(ovflag[:], psA[0:3 * E, 2, 0:1], ovbase[0:3 * E], None, ALU.is_gt))
        v.tensor_copy(ovpre[:], ovflag[:]).then_inc(flag_ready, 1)
        dve.wait_ge(pre_done, 1)
        seq.link(v.tensor_copy(ovpre[:], psA[0:3 * E, 2, 1:2]))
        v.tensor_scalar(ovhot[:], iota[0:3 * E, 0:OVMAX], ovpre[:], ovflag[:], ALU.is_equal,
                        ALU.mult).then_inc(ovhot_ready, 1)
        dve.wait_ge(ovlist_done, 1)
        v.tensor_copy(ovtab[:], psA[0:1, 3, 0:2 * OVMAX + 1]).then_inc(routed, 1)

        def turned_lo(hi_sem, count, hi, lo, sem):
            dve.wait_ge(hi_sem, count)
            ps = psT.rearrange("p b (k c) -> p (b k) c", k=4)
            v.tensor_tensor(lo[:], ps, hi[:].bitcast(F32), ALU.subtract).then_inc(sem, 1)

        def swiglu_in(i):
            dve.wait_ge(gu_done, i + 1)
            v.tensor_scalar(gate_t[:], psA[:, 0:2, :].rearrange("p b c -> p (b c)"), LIMIT, None,
                            ALU.min).then_inc(gate_min, 1)
            v.tensor_scalar(up_t[:], psA[:, 2:4, :].rearrange("p b c -> p (b c)"), LIMIT, -LIMIT, ALU.min,
                            ALU.max)

        def swiglu_out(i, chain):
            dve.wait_ge(sig_done, i + 1)
            dve.wait_ge(gate_min, i + 1)
            chain.link(v.tensor_tensor(gate_t[:], gate_t[:], act_t[:], ALU.mult))
            v.scalar_tensor_tensor(act_t[:], up_t[:], 1.0, gate_t[:], ALU.add, ALU.mult).then_inc(act_ready, 1)

        for c in range(XSPL):
            expert_lo(0, c, c)
        turned_lo(xT_hi_s, 1, xT_hi, xT_lo, xT_lo_s)
        slot_rows(slice(1, 2), iota[:, 0:P])
        shift_queue(seq)
        take_table(1, seq)
        slot_rows(slice(2, 3), iota[:, 0:P])
        for c in range(XSPL, GUC):
            expert_lo(0, c, c % XRAW)
        shift_queue(seq)
        take_table(2, seq)
        swiglu_in(0)
        turned_lo(xT_hi_s, 2, xT_hi, xT_lo, xT_lo_s)
        expert_lo(1, 0, body_slot(0))
        swiglu_out(0, seq)
        for c in range(1, XSPL):
            expert_lo(1, c, body_slot(c))
        seq.join()
        start = seq.used

        def body(i, last, chain):
            slot_rows(bass.ds(i + 2, 1), iota[:, 0:P])
            for c in range(XSPL, GUC):
                expert_lo(i, c, body_slot(c))
            if not (isinstance(i, int) and i == 1):
                dve.wait_ge(y_out, 16 * (i - 1))
            shift_queue(chain)
            take_table(i + 2, chain)
            swiglu_in(i)
            turned_lo(xT_hi_s, i + 2, xT_hi, xT_lo, xT_lo_s)
            if not last:
                expert_lo(i + 1, 0, body_slot(0))
            swiglu_out(i, chain)
            if not last:
                for c in range(1, XSPL):
                    expert_lo(i + 1, c, body_slot(c))

        body(1, False, seq)
        assert seq.used == start + DVE_BODY_LINKS
        with dve.Fori(2, E - 1) as i:
            chain = Steps(dve, dve_seq, start + DVE_BODY_LINKS * (i - 1))
            body(i, False, chain)
            body_used = chain.used
        assert body_used == DVE_BODY_LINKS, body_used
        seq.used = start + body_used * (E - 2)
        body(E - 1, True, seq)
        dve.wait_ge(y_out, 16 * (E - 1))
        shift_queue(seq)
        v.tensor_scalar(didx[:], queue[:, 0, 0:1], BIG, None, ALU.add).then_inc(tab_ready, 1)
        start = seq.used
        count = dve.value_load(ovtab[0:1, 2 * OVMAX:2 * OVMAX + 1], min_val=0, max_val=OVMAX)
        with dve.If(count > 0):
            with dve.Fori(0, count) as j:
                chain = Steps(dve, dve_seq, start + DVE_OV_LINKS * j)
                e = dve.value_load(ovtab[0:1, bass.ds(j, 1)], min_val=0, max_val=E - 1)
                first = dve.value_load(ovtab[0:1, bass.ds(j + OVMAX, 1)], min_val=P, max_val=3 * P)
                dve.wait_ge(y_out, 16 * (E + j))
                slot_rows(bass.ds(e, 1), iota[:, bass.ds(first, P)])
                dve.wait_ge(tab_done, E + 3 + j)
                chain.link(v.tensor_copy(queue[:, 0, :], psD[:, 0, 1:3]))
                v.tensor_scalar(didx[:], queue[:, 0, 0:1], BIG, None, ALU.add)
                v.tensor_scalar(gidx[:], psD[:, 0, 0:1], BIG, None, ALU.add).then_inc(tab_ready, 1)
                turned_lo(xT_hi_s, E + 2 + j, xT_hi, xT_lo, xT_lo_s)
                for c in range(GUC):
                    expert_lo(E + j, c, c % XRAW)
                swiglu_in(E + j)
                swiglu_out(E + j, chain)
                dve.wait_ge(y_out, 16 * (E + j + 1))
                ov_used = chain.used
        assert ov_used == DVE_OV_LINKS, ov_used

        dve.wait_ge(y_out, 16 * E)
        dve.wait_ge(dn_done, E)
        v.tensor_copy(smax, smax).then_inc(fin_ready, 1)
        dve.wait_ge(lnffn_in, 32)
        fin = Steps(dve, fin_seq, 0)
        for t in range(TT):
            dve.wait_ge(yrows_in[t], 16)
            row = h2[:, t, :]
            y = yrows[:, t, :].rearrange("p (k d) -> p k d", k=TOPK)
            fin.link(v.scalar_tensor_tensor(row, row, ALPHA, y[:, 0, :], ALU.mult, ALU.add))
            for k in range(1, TOPK):
                fin.link(v.tensor_tensor(row, row, y[:, k, :], ALU.add))
            norm_stats(t, row, fin)
        for t in range(TT):
            norm_apply(2 * TT + t, t, h2[:, t, :], lnffn_g[:], lnffn_b[:], fin).then_inc(fin_ready, 1)

    @block.tensor
    def _(pe):
        mm = nc.tensor.matmul

        def passes(dst, stat, mov, first, last):
            (sh, sl), (mh, ml) = stat, mov
            mm(dst, sh, mh, start=first, stop=False)
            mm(dst, sh, ml, start=False, stop=False)
            return mm(dst, sl, mh, start=False, stop=last)

        def turn(dst, src, done, count_tiles=KT):
            for k in range(count_tiles):
                ins = nc.tensor.transpose(dst[:, k // 4, (k % 4) * P:(k % 4 + 1) * P], src[:, k * P:(k + 1) * P],
                                          ident[:])
            ins.then_inc(done, 1)

        pe.wait_ge(const_ready, build.const_total)
        for t in range(TT):
            pe.wait_ge(h_norm, t + 1)
            if t >= 2:
                pe.wait_ge(hT_hi_s, t - 1)
                pe.wait_ge(hT_lo_s, t - 1)
            turn(psX[:, 2 * (t % 2):2 * (t % 2) + 2, :], xt[:, t, :], h_turned)

        def chunk_half(c, half):
            kind, j = DENSE[c][:2]
            bank = 2 * (c % 2) + half
            split = c in SPLIT_AT
            rs, ss = c % RAW, SPLIT_AT.get(c, 0) % SPL
            if half == 0:
                if split:
                    pe.wait_ge(hi_ready, SPLIT_AT[c] + 1)
                    pe.wait_ge(lo_ready, SPLIT_AT[c] + 1)
                else:
                    raw_wait(pe, c)
                if c >= 2:
                    pe.wait_ge(evac_sem(c - 2), evac_count(c - 2))
                if kind == "gp" and j == 0:
                    pe.wait_ge(gla_out, GH)
                if kind == "fp" and j == 0:
                    pe.wait_ge(fox_hi, 4)
                    pe.wait_ge(fox_lo, 4)
            rawv = raw[:, rs, :].rearrange("p (k c) -> p k c", k=KT)
            hiv = whi[:, ss, :].rearrange("p (k c) -> p k c", k=KT)
            lov = wlo[:, ss, :].rearrange("p (k c) -> p k c", k=KT)
            if kind in BY_TOKEN:
                for u in range(2):
                    t = 2 * half + u
                    if c == 0:
                        pe.wait_ge(hT_hi_s, t + 1)
                        pe.wait_ge(hT_lo_s, t + 1)
                    dst = psA[:, bank, u * CW:(u + 1) * CW]
                    tok = slice(t * P, (t + 1) * P)
                    for k in range(KT):
                        ins = passes(dst, (hT_hi[:, k, tok], hT_lo[:, k, tok]), (hiv[:, k, :], lov[:, k, :]),
                                     k == 0, k == KT - 1)
            else:
                dst = psA[:, bank, :]
                col = slice(half * P, (half + 1) * P)
                for k in range(KT):
                    if split:
                        ins = passes(dst, (hiv[:, k, col], lov[:, k, col]), (hT_hi[:, k, :], hT_lo[:, k, :]),
                                     k == 0, k == KT - 1)
                    else:
                        ins = mm(dst, rawv[:, k, col], gr[:, k, :], start=k == 0, stop=k == KT - 1)
            ins.then_inc(half_done, 1)

        def hook(s):
            if s == 1:
                pe.wait_ge(small_hi, 1)
                pe.wait_ge(small_lo, 1)
                n = RANK + FH
                for t in range(TT):
                    tok = slice(t * P, (t + 1) * P)
                    for k in range(KT):
                        ins = passes(psX[:, 2, t * n:(t + 1) * n], (hT_hi[:, k, tok], hT_lo[:, k, tok]),
                                     (sm_hi[:, k, :], sm_lo[:, k, :]), k == 0, k == KT - 1)
                ins.then_inc(small_done, 1)
            if s == 2:
                pe.wait_ge(small_evac, 1)
                for t in range(TT):
                    ins = mm(psX[0:RANK, 3, t * P:(t + 1) * P], glf[:, t, 0:RANK], ident[:], start=True, stop=True)
                ins.then_inc(glT_done, 1)
            if s in (3, 4):
                if s == 3:
                    pe.wait_ge(glT_evac, 1)
                    pe.wait_ge(params_in, 96)
                for t in (2 * (s - 3), 2 * (s - 3) + 1):
                    mm(psX[:, t, :], glT[:, t * P:(t + 1) * P], w_up[:], start=True, stop=True).then_inc(gate_pre, 1)
            if s in (5, 6):
                pe.wait_ge(la_ready, TT)
                for t in (2 * (s - 5), 2 * (s - 5) + 1):
                    mm(psX[:, t, :], suffix[:], la[:, t, :], start=True, stop=True).then_inc(suf_done, 1)
            if s == 7:
                pe.wait_ge(kd_mul, TT)
                for h in range(GH):
                    for t in range(TT):
                        o = h * NCH + 2 * t
                        ins = mm(psX[:, 0, o:o + 2], la[:, t, h * GDK:(h + 1) * GDK], chunk_sel, start=True, stop=True)
                ins.then_inc(tot_done, 1)
            if GLA0 <= s < GLA0 + 3 * GH:
                h, part = divmod(s - GLA0, 3)
                if part == 0:
                    if h == 0:
                        pe.wait_ge(dec_ready, 1)
                        pe.wait_ge(kd_mul, TT)
                        pe.wait_ge(act_half, 2 * 8)
                    else:
                        pe.wait_ge(gla_out, h)
                    for n in range(NCH):
                        rows = slice(CHUNK * (n % 2), CHUNK * (n % 2 + 1))
                        ins = mm(chunk_state(n),
                                 gk[rows, n // 2, h * GDK:(h + 1) * GDK], gv[rows, n // 2, h * GDV:(h + 1) * GDV],
                                 start=True, stop=True)
                    ins.then_inc(ds_done, 1)
                if part == 1:
                    pe.wait_ge(st_ready, h + 1)
                    for half in range(2):
                        for n in range(NCH):
                            tok = slice(CHUNK * n, CHUNK * (n + 1))
                            ins = mm(psX[:, half, tok], state[:, n, half * P:(half + 1) * P], gq[:, h, tok],
                                     start=True, stop=True)
                    ins.then_inc(go_done, 1)
                if part == 2:
                    pe.wait_ge(gsq_done, h + 1)
                    for half in range(2):
                        ins = mm(psX[:, 2, :], ones_dv[:], osq[:, half, :], start=half == 0, stop=half == 1)
                    ins.then_inc(gms_done, 1)
            if s == FSLOT:
                pe.wait_ge(lsf_ready, 1)
                pe.wait_ge(gla_out, GH)
                for t in range(TT):
                    for u in range(t + 1):
                        tri = incl if u == t else ones
                        mm(psX[:, 0, t * FH:(t + 1) * FH], tri[:], lsf[:, u, :], start=u == 0, stop=u == t)
                for r in range(2):
                    for t in range(TT):
                        for u in range(t + 1):
                            tri = incl if u == t else ones
                            ins = mm(psX[32 * r:32 * r + FH, 1, t * P:(t + 1) * P], lsf[:, u, :], tri[:],
                                     start=u == 0, stop=u == t)
                ins.then_inc(f_done, 1)
            q = s - ATT0
            if 2 <= q < ATT_SLOTS + 2:
                for b, (h, t) in enumerate(attention_tiles(q - 2)):
                    pe.wait_ge(at_probT, 2 * (q - 2) + b + 1)
                    for u in range(t + 1):
                        ins = mm(psX[:, 2 + b, 0:P], fv[:, h, u, :], probsT[:, b, u * P:(u + 1) * P],
                                 start=u == 0, stop=u == t)
                    ins.then_inc(at_out, 1)
            if 0 <= q < ATT_SLOTS:
                if q == 0:
                    pe.wait_ge(f_evac, 1)
                    pe.wait_ge(fneg_lo, 1)
                if q % 4 == 0:
                    pe.wait_ge(act_half, 2 * (18 + 2 * (q // 4)))
                for b, (h, t) in enumerate(attention_tiles(q)):
                    n = P * (t + 1)
                    if q >= 1:
                        pe.wait_ge(at_max, 2 * (q - 1) + b + 1)
                    qk = fqk[(h // 2) % 2]
                    mm(psX[:, b, 0:n], qk[:, 0, h % 2, t * P:(t + 1) * P], qk[:, 1, h % 2, 0:n], start=True, stop=False)
                    mm(psX[:, b, 0:n], sel[:, h * P:(h + 1) * P], fneg[:, 0:n], start=False, stop=False)
                    mm(psX[:, b, t * P:n], ident_b[:], negmask[:], start=False, stop=True).then_inc(at_score, 1)
            if 1 <= q < ATT_SLOTS + 1:
                for b, (h, t) in enumerate(attention_tiles(q - 1)):
                    pe.wait_ge(at_prob, 2 * (q - 1) + b + 1)
                    if q >= 2:
                        pe.wait_ge(at_evac, 2 * (q - 2) + b + 1)
                    for u in range(t + 1):
                        ins = nc.tensor.transpose(psX[:, 2 + b, u * P:(u + 1) * P], probs[:, b, u * P:(u + 1) * P],
                                                  ident[:])
                    ins.then_inc(at_turn, 1)

        for c in range(NCD):
            for half in range(2):
                chunk_half(c, half)
                hook(2 * c + half)

        def turn_h2(t):
            pe.wait_ge(h2_norm, t + 1)
            if t >= 2:
                pe.wait_ge(h2T_evac, t - 1)
            turn(psX[:, 2 * (t % 2):2 * (t % 2) + 2, :], h2[:, t, :], h2_turned)

        pe.wait_ge(dve_half, 2 * (NCD - NPROJ))
        for t in range(TT):
            if t >= 2:
                pe.wait_ge(wo_evac, t - 1)
            for j in range(4):
                if t == 0:
                    raw_wait(pe, NCD + j)
                w = raw[:, (NCD + j) % RAW, :].rearrange("p (k c) -> p k c", k=KT)
                dst = psA[:, 2 * (t % 2) + j // 2, (j % 2) * CW:(j % 2 + 1) * CW]
                for k in range(KT):
                    ins = mm(dst, mix[:, k, t * P:(t + 1) * P], w[:, k, :], start=k == 0, stop=k == KT - 1)
            ins.then_inc(wo_done, 1)
            if t >= 2:
                turn_h2(t - 2)
        turn_h2(TT - 2)
        for t in range(TT):
            if t == TT - 1:
                turn_h2(t)
            pe.wait_ge(h2T_evac, t + 1)
            if t == 0:
                pe.wait_ge(wo_evac, TT - 1)
            for k in range(KT):
                ins = mm(psA[:, 0, t * E:(t + 1) * E], h2T[:, k, t * P:(t + 1) * P], w_rt[:, k, :], start=k == 0,
                         stop=k == KT - 1)
            ins.then_inc(lg_done, 1)
        pe.wait_ge(mem_ready, 1)
        for t in range(TT):
            for u in range(t + 1):
                tri = strict if u == t else ones
                mm(psA[:, 1, t * E:(t + 1) * E], tri[:], member3[:, u, 0:E], start=u == 0, stop=u == t)
        for t in range(TT):
            ins = mm(psA[0:3 * E, 2, 0:1], member3[:, t, :], ones[:, 0:1], start=t == 0, stop=t == TT - 1)
        ins.then_inc(pos_done, 1)

        def table(x, e):
            pe.wait_ge(slot_ready, x + 1)
            for t in range(TT):
                ins = mm(psD[:, 0, 0:4], slots[:, t, :], vals[:, t, e, :], start=t == 0, stop=t == TT - 1)
            ins.then_inc(tab_done, 1)

        table(0, 0)
        pe.wait_ge(flag_ready, 1)
        mm(psA[0:3 * E, 2, 1:2], strict[0:3 * E, 0:3 * E], ovflag[:], start=True, stop=True).then_inc(pre_done, 1)
        pe.wait_ge(ovhot_ready, 1)
        mm(psA[0:1, 3, 0:OVMAX], ovexp[0:3 * E], ovhot[:], start=True, stop=True)
        mm(psA[0:1, 3, OVMAX:2 * OVMAX], ovbase[0:3 * E], ovhot[:], start=True, stop=True)
        mm(psA[0:1, 3, 2 * OVMAX:2 * OVMAX + 1], ovflag[:], ones[0:3 * E, 0:1], start=True,
           stop=True).then_inc(ovlist_done, 1)

        def gate_up(i, c):
            pe.wait_ge(hi_ready, NS + GUC * i + c + 1)
            pe.wait_ge(lo_ready, NS + GUC * i + c + 1)
            hi, lo = xsplit(c)
            for n in range(4):
                cols = slice(n * 512, (n + 1) * 512)
                ins = passes(psA[:, n, :], (xT_hi[:, c, :], xT_lo[:, c, :]), (hi[:, cols], lo[:, cols]), c == 0, False)
            ins.then_inc(gu_used, 1)

        def gate_up_bias(i):
            pe.wait_ge(bgu_in, 16 * (i + 1))
            for n in range(4):
                ins = mm(psA[:, n, :], ones_r[:], bgu[:, n * 512:(n + 1) * 512], start=False, stop=True)
            ins.then_inc(gu_done, 1)

        def down(q, slot, uses):
            xraw_wait(pe, slot, uses)
            for kk in range(2):
                k = 2 * q + kk
                for n in range(2):
                    cols = slice(kk * D + n * 512, kk * D + (n + 1) * 512)
                    ins = mm(psD[:, n, :], aT[:, k, :], xraw(slot)[:, cols], start=k == 0, stop=False)
            ins.then_inc(dn_used, 1)

        def down_bias(i):
            pe.wait_ge(bdn_in, 16 * (i + 1))
            for n in range(2):
                ins = mm(psD[:, n, :], ones_r[:], bdn[:, n * 512:(n + 1) * 512], start=False, stop=True)
            ins.then_inc(dn_done, 1)

        def turn_x(x):
            pe.wait_ge(xg_in, 16 * (x + 1))
            turn(psT, xg, xt_done)

        def turn_a(i, x):
            pe.wait_ge(act_ready, i + 1)
            pe.wait_ge(xT_lo_s, x + 1)
            turn(psT, act_t, aturn_done)

        def split_ready(hi_sem, lo_sem, n):
            pe.wait_ge(hi_sem, n)
            pe.wait_ge(lo_sem, n)

        turn_x(0)
        split_ready(xT_hi_s, xT_lo_s, 1)
        pe.wait_ge(routed, 1)
        for c in range(GUC):
            gate_up(0, c)
            if c == 0:
                table(1, 1)
            if c == GUC - 2:
                pe.wait_ge(tab_ready, 2)
                table(2, 2)
        gate_up_bias(0)
        turn_x(1)
        turn_a(0, 1)
        def body(i):
            split_ready(xT_hi_s, xT_lo_s, i + 1)
            for c in range(GUC):
                gate_up(i, c)
                if c == GUC - 2:
                    pe.wait_ge(tab_ready, i + 2)
                    if not (isinstance(i, int) and i == 1):
                        pe.wait_ge(y_ready, i - 1)
                    table(i + 2, bass.ds(i + 2, 1))
            gate_up_bias(i)
            pe.wait_ge(aT_ready, i)
            turn_x(i + 1)
            pe.wait_ge(tab_ready, i + 3)
            for q in range(DNC):
                down(q, body_slot(GUC + q), body_uses(i, GUC + q))
            down_bias(i - 1)
            turn_a(i, i + 1)

        body(1)
        with pe.Fori(2, E) as i:
            body(i)
        pe.wait_ge(aT_ready, E)
        pe.wait_ge(y_ready, E - 1)
        for q in range(DNC):
            down(q, body_slot(q), body_uses(E, q))
        down_bias(E - 1)
        count = pe.value_load(ovtab[0:1, 2 * OVMAX:2 * OVMAX + 1], min_val=0, max_val=OVMAX)
        with pe.If(count > 0):
            with pe.Fori(0, count) as j:
                e = pe.value_load(ovtab[0:1, bass.ds(j, 1)], min_val=0, max_val=E - 1)
                pe.wait_ge(y_ready, E + j)
                table(E + 2 + j, bass.ds(e, 1))
                turn_x(E + 1 + j)
                split_ready(xT_hi_s, xT_lo_s, E + 2 + j)
                for c in range(GUC):
                    gate_up(E + j, c)
                gate_up_bias(E + j)
                turn_a(E + j, E + 1 + j)
                pe.wait_ge(aT_ready, E + 1 + j)
                for q in range(DNC):
                    down(q, (GUC + q) % XRAW, NMAIN // XRAW + BODY_USES * j + (GUC + q) // XRAW + 1)
                down_bias(E + j)

    block.__exit__(None, None, None)


_INS = ['x', 'ln_in_g', 'ln_in_b', 'w_in', 'w_gla_gate_up', 'b_gla_gate', 'g_gla_norm', 'b_forget', 'w_gla_proj',
        'w_fox_proj', 'w_out', 'ln_mix_g', 'ln_mix_b', 'w_router', 'b_router', 'w_gate_up', 'b_gate_up', 'w_down',
        'b_down', 'ln_ffn_g', 'ln_ffn_b']


def kernel(**inputs):
    import concourse.bacc as bacc
    from concourse.bass_utils import run_bass_kernel_spmd

    nc = bacc.Bacc("TRN2", target_bir_lowering=False, num_devices=1)
    arrays, args = {}, {}
    for name in _INS:
        array = np.ascontiguousarray(inputs[name])
        arrays[f"in_{name}"] = array
        args[name] = nc.dram_tensor(f"in_{name}", array.shape, mybir.dt.from_np(array.dtype),
                                    kind="ExternalInput").ap()
    out = nc.dram_tensor("out_h", (1, T, D), F32, kind="ExternalOutput").ap()
    build(nc, args, out)
    result = run_bass_kernel_spmd(nc, [arrays], core_ids=[0])
    return result.results[0]["out_h"]
```
